# Optimizing a Trainium2 kernel written in Bass

```python
import jax
import jax.numpy as jnp
from jax import lax
import numpy as np

D_MODEL = 2048
BATCH = 1
SEQ = 256
DEPTH = 2

CHUNK = 64
N_MEM = 256
EPS = 1e-6
MEM_WIDTH = D_MODEL // 4
TOKEN_WIDTH = D_MODEL - MEM_WIDTH
M_HEADS = 4
M_HEAD_DIM = MEM_WIDTH // M_HEADS
A_HEAD_DIM = 64
A_Q_HEADS = TOKEN_WIDTH // A_HEAD_DIM
A_KV_HEADS = A_Q_HEADS // 8
A_GROUP = A_Q_HEADS // A_KV_HEADS
WINDOW = 128
WINDOW_CHUNKS = -(-WINDOW // CHUNK)
ROPE_THETA = 500000.0
ROT_DIM = A_HEAD_DIM // 4
B_KEY_DIM = 128
B_HEADS = TOKEN_WIDTH // B_KEY_DIM
B_VAL_DIM = TOKEN_WIDTH // B_HEADS
SUB = 16
D_FF = -(-(8 * D_MODEL) // (3 * 256)) * 256
N_A_LAYERS = (DEPTH + 1) // 2
N_B_LAYERS = DEPTH // 2
A_SPLITS = (A_Q_HEADS * A_HEAD_DIM, A_KV_HEADS * A_HEAD_DIM, A_KV_HEADS * A_HEAD_DIM, MEM_WIDTH)
B_SPLITS = (B_HEADS * B_KEY_DIM, B_HEADS * B_KEY_DIM, B_HEADS * B_VAL_DIM, B_HEADS * B_VAL_DIM, MEM_WIDTH)

kernel_name = "hybrid_swa_sink_hgrn2_memory_trunk"

def _split(t, sizes):
    return jnp.split(t, np.cumsum(sizes)[:-1].tolist(), axis=-1)

def rms_norm(x, g):
    xf = x.astype(jnp.float32)
    y = xf * lax.rsqrt(jnp.mean(xf * xf, axis=-1, keepdims=True) + EPS)
    return (y * g.astype(jnp.float32)).astype(x.dtype)

def partial_rope(x, positions):
    half = ROT_DIM // 2
    inv_freq = ROPE_THETA ** (-jnp.arange(half, dtype=jnp.float32) / half)
    ang = positions.astype(jnp.float32)[..., None] * inv_freq
    cos = jnp.cos(ang)[:, :, None, :]
    sin = jnp.sin(ang)[:, :, None, :]
    xr = x[..., :ROT_DIM].astype(jnp.float32)
    x1, x2 = xr[..., :half], xr[..., half:]
    rot = jnp.concatenate([x1 * cos - x2 * sin, x2 * cos + x1 * sin], axis=-1)
    return jnp.concatenate([rot.astype(x.dtype), x[..., ROT_DIM:]], axis=-1)

def _band(t, n_chunks):
    parts = [jnp.pad(t, ((0, 0), (n, 0), (0, 0), (0, 0), (0, 0)))[:, :n_chunks]
             for n in range(WINDOW_CHUNKS - 1, -1, -1)]
    return jnp.concatenate(parts, axis=2)

def swa_sink_attention(q, k, v, sinks):
    bsz, seq = q.shape[0], q.shape[1]
    n_chunks = seq // CHUNK
    kw = WINDOW_CHUNKS * CHUNK
    qc = q.reshape(bsz, n_chunks, CHUNK, A_KV_HEADS, A_GROUP, A_HEAD_DIM)
    kb = _band(k.reshape(bsz, n_chunks, CHUNK, A_KV_HEADS, A_HEAD_DIM), n_chunks)
    vb = _band(v.reshape(bsz, n_chunks, CHUNK, A_KV_HEADS, A_HEAD_DIM), n_chunks)
    s = jnp.einsum('bcqhgd,bckhd->bhgcqk', qc, kb).astype(jnp.float32) * (A_HEAD_DIM ** -0.5)
    key_chunk = jnp.arange(n_chunks)[:, None] - (WINDOW_CHUNKS - 1) + jnp.arange(kw)[None, :] // CHUNK
    valid = (key_chunk >= 0)[None, None, None, :, None, :]
    s = jnp.where(valid, s, -jnp.inf)
    sink = sinks.astype(jnp.float32).reshape(A_KV_HEADS, A_GROUP)[None, :, :, None, None, None]
    m = jnp.maximum(jnp.max(s, axis=-1, keepdims=True), sink)
    p = jnp.exp(s - m)
    p = p / (jnp.sum(p, axis=-1, keepdims=True) + jnp.exp(sink - m))
    o = jnp.einsum('bhgcqk,bckhd->bcqhgd', p.astype(v.dtype), vb)
    return o.reshape(bsz, seq, A_Q_HEADS * A_HEAD_DIM)

def hgrn2_chunkwise(q, k, v, log_f):
    bsz, seq, nh, dk = q.shape
    dv = v.shape[-1]
    n_chunks = seq // CHUNK
    n_sub = CHUNK // SUB

    def to_chunks(t):
        return t.reshape(bsz, n_chunks, CHUNK, nh, t.shape[-1]).transpose(1, 0, 3, 2, 4)

    earlier = (jnp.arange(CHUNK)[None, :] // SUB) < jnp.arange(n_sub)[:, None]
    causal_sub = jnp.tril(jnp.ones((SUB, SUB), dtype=bool))

    def step(state, inp):
        qc, kc, vc, gc = inp
        b = jnp.cumsum(gc, axis=2)
        o_inter = jnp.einsum('bhtk,bhkv->bhtv', qc * jnp.exp(b), state)
        bs = b.reshape(bsz, nh, n_sub, SUB, dk)
        r = jnp.concatenate([jnp.zeros((bsz, nh, 1, dk), b.dtype), bs[:, :, :-1, -1]], axis=2)
        qs = qc.reshape(bsz, nh, n_sub, SUB, dk)
        ks = kc.reshape(bsz, nh, n_sub, SUB, dk)
        vs = vc.reshape(bsz, nh, n_sub, SUB, dv)
        q_rel = qs * jnp.exp(bs - r[:, :, :, None, :])
        k_dec = jnp.where(earlier[None, None, :, :, None], r[:, :, :, None, :] - b[:, :, None, :, :], -jnp.inf)
        k_rel = kc[:, :, None] * jnp.exp(k_dec)
        a_off = jnp.einsum('bhntk,bhnsk->bhnts', q_rel, k_rel)
        diff = bs[:, :, :, :, None, :] - bs[:, :, :, None, :, :]
        diff = jnp.where(causal_sub[None, None, None, :, :, None], diff, -jnp.inf)
        a_diag = jnp.einsum('bhntk,bhnsk,bhntsk->bhnts', qs, ks, jnp.exp(diff))
        o_intra = (jnp.einsum('bhnts,bhsv->bhntv', a_off, vc)
                   + jnp.einsum('bhnts,bhnsv->bhntv', a_diag, vs))
        o = o_inter + o_intra.reshape(bsz, nh, CHUNK, dv)
        b_last = b[:, :, -1:, :]
        new_state = (jnp.exp(b_last[:, :, 0, :])[..., None] * state
                     + jnp.einsum('bhsk,bhsv->bhkv', kc * jnp.exp(b_last - b), vc))
        return new_state, o

    state0 = jnp.zeros((bsz, nh, dk, dv), jnp.float32)
    _, outs = lax.scan(step, state0, (to_chunks(q), to_chunks(k), to_chunks(v), to_chunks(log_f)))
    return outs.transpose(1, 0, 3, 2, 4).reshape(bsz, seq, nh, dv)

def memory_attention(q, mem_k, mem_v):
    s = jnp.einsum('bshd,bmhd->bhsm', q, mem_k).astype(jnp.float32) * (M_HEAD_DIM ** -0.5)
    p = jax.nn.softmax(s, axis=-1)
    o = jnp.einsum('bhsm,bmhd->bshd', p.astype(mem_v.dtype), mem_v)
    return o.reshape(q.shape[0], q.shape[1], MEM_WIDTH)

def setup_inputs(seed: int = 0) -> dict:
    key = jax.random.key(seed)
    ks = jax.random.split(key, 24)

    def nrm(k, shape, scale):
        return jax.random.normal(k, shape, jnp.float32) * scale

    def gain(k, shape):
        return 1.0 + 0.02 * jax.random.normal(k, shape, jnp.float32)

    offsets = jax.random.randint(ks[2], (BATCH, 1), 0, 1024, dtype=jnp.int32)
    return {
        "x": nrm(ks[0], (BATCH, SEQ, D_MODEL), 1.0),
        "mem": nrm(ks[1], (BATCH, N_MEM, D_MODEL), 1.0),
        "positions": offsets + jnp.arange(SEQ, dtype=jnp.int32)[None, :],
        "norm_mix": gain(ks[3], (DEPTH, D_MODEL)),
        "norm_ffn": gain(ks[4], (DEPTH, D_MODEL)),
        "norm_mem": gain(ks[5], (DEPTH, D_MODEL)),
        "w_in_a": nrm(ks[6], (N_A_LAYERS, D_MODEL, sum(A_SPLITS)), D_MODEL ** -0.5),
        "q_norm_a": gain(ks[7], (N_A_LAYERS, A_HEAD_DIM)),
        "k_norm_a": gain(ks[8], (N_A_LAYERS, A_HEAD_DIM)),
        "sinks_a": nrm(ks[9], (N_A_LAYERS, A_Q_HEADS), 1.0),
        "w_in_b": nrm(ks[10], (N_B_LAYERS, D_MODEL, sum(B_SPLITS)), D_MODEL ** -0.5),
        "lb_logits": nrm(ks[11], (DEPTH, B_HEADS * B_KEY_DIM), 0.1),
        "g_norm_b": gain(ks[12], (N_B_LAYERS, B_VAL_DIM)),
        "w_mem_kv": nrm(ks[13], (DEPTH, D_MODEL, 2 * MEM_WIDTH), D_MODEL ** -0.5),
        "q_norm_m": gain(ks[14], (DEPTH, M_HEAD_DIM)),
        "k_norm_m": gain(ks[15], (DEPTH, M_HEAD_DIM)),
        "w_o": nrm(ks[16], (DEPTH, TOKEN_WIDTH + MEM_WIDTH, D_MODEL), (TOKEN_WIDTH + MEM_WIDTH) ** -0.5),
        "w_gate_up": nrm(ks[17], (DEPTH, D_MODEL, 2 * D_FF), D_MODEL ** -0.5),
        "w_down": nrm(ks[18], (DEPTH, D_FF, D_MODEL), D_FF ** -0.5),
    }

def reference(x, mem, positions, norm_mix, norm_ffn, norm_mem, w_in_a, q_norm_a, k_norm_a, sinks_a,
              w_in_b, lb_logits, g_norm_b, w_mem_kv, q_norm_m, k_norm_m, w_o, w_gate_up, w_down):
    bsz, seq = x.shape[0], x.shape[1]
    lb_soft = jax.nn.softmax(lb_logits.astype(jnp.float32), axis=0)
    lower_bounds = jnp.cumsum(lb_soft, axis=0) - lb_soft[0:1]
    for i in range(DEPTH):
        j = i // 2
        h = rms_norm(x, norm_mix[i])
        mem_kv = rms_norm(mem, norm_mem[i]) @ w_mem_kv[i]
        mem_k, mem_v = _split(mem_kv, (MEM_WIDTH, MEM_WIDTH))
        mem_k = rms_norm(mem_k.reshape(bsz, -1, M_HEADS, M_HEAD_DIM), k_norm_m[i])
        mem_v = mem_v.reshape(bsz, -1, M_HEADS, M_HEAD_DIM)
        if i % 2 == 0:
            q_a, k_a, v_a, q_m = _split(h @ w_in_a[j], A_SPLITS)
            q_a = partial_rope(rms_norm(q_a.reshape(bsz, seq, A_Q_HEADS, A_HEAD_DIM), q_norm_a[j]), positions)
            k_a = partial_rope(rms_norm(k_a.reshape(bsz, seq, A_KV_HEADS, A_HEAD_DIM), k_norm_a[j]), positions)
            v_a = v_a.reshape(bsz, seq, A_KV_HEADS, A_HEAD_DIM)
            mix = swa_sink_attention(q_a, k_a, v_a, sinks_a[j])
        else:
            q_b, f_b, i_b, g_b, q_m = _split(h @ w_in_b[j], B_SPLITS)
            lb = lower_bounds[i]
            z = f_b.astype(jnp.float32)
            log_f = jnp.logaddexp(jnp.log(lb), jnp.log1p(-lb) + jax.nn.log_sigmoid(z))
            k_b = (1.0 - lb) * jax.nn.sigmoid(-z)
            shp_k = (bsz, seq, B_HEADS, B_KEY_DIM)
            shp_v = (bsz, seq, B_HEADS, B_VAL_DIM)
            o_b = hgrn2_chunkwise(jax.nn.silu(q_b.astype(jnp.float32)).reshape(shp_k), k_b.reshape(shp_k),
                                  i_b.astype(jnp.float32).reshape(shp_v), log_f.reshape(shp_k))
            o_b = rms_norm(o_b.astype(x.dtype), g_norm_b[j]) * jax.nn.silu(g_b.reshape(shp_v))
            mix = o_b.reshape(bsz, seq, B_HEADS * B_VAL_DIM)
        q_m = rms_norm(q_m.reshape(bsz, seq, M_HEADS, M_HEAD_DIM), q_norm_m[i])
        mem_out = memory_attention(q_m, mem_k, mem_v)
        x = x + jnp.concatenate([mix, mem_out], axis=-1) @ w_o[i]
        gate, up = _split(rms_norm(x, norm_ffn[i]) @ w_gate_up[i], (D_FF, D_FF))
        x = x + (jax.nn.silu(gate) * up) @ w_down[i]
    return x


_drawn_inputs = setup_inputs


def setup_inputs(seed=0):
    import zlib

    import numpy as np

    out = dict(_drawn_inputs(seed))
    spreads = {}
    factors = {'norm_mix': 3.971,
     'norm_ffn': 2.701,
     'norm_mem': 8.0,
     'q_norm_a': 8.0,
     'k_norm_a': 8.0,
     'sinks_a': 8.0,
     'lb_logits': 8.0,
     'g_norm_b': 7.029,
     'q_norm_m': 8.0,
     'k_norm_m': 8.0}
    for name, (base, spread) in spreads.items():
        noise = np.random.default_rng([zlib.crc32(name.encode()), seed]).standard_normal(out[name].shape)
        drawn = base * np.exp(spread * noise) if base else spread * noise
        out[name] = jnp.asarray(drawn.astype(out[name].dtype))
    for name, factor in factors.items():
        out[name] = (out[name] * factor).astype(out[name].dtype)
    return out
```

```python
from contextlib import ExitStack, contextmanager

import numpy as np
import concourse.bass as bass
from concourse import mybir

F32 = mybir.dt.float32
F32R = mybir.dt.float32r
I32 = mybir.dt.int32
ALU = mybir.AluOpType
ACT = mybir.ActivationFunctionType
AX = mybir.AxisListType

P = 128
TILES = 2
SEQ = TILES * P
D = 2048
KT = D // P
COLS = 512
BLOCKS = D // COLS
D_FF = 5632
FT = D_FF // P
CHUNKS_FF = D_FF // COLS
N_MEM = 256
HD_A, KV_A, GROUP_A = 64, 3, 8
HD_B, HEADS_B = 128, 12
GROUPS = 3
TOKEN_WIDTH = 1536
ROT = 8
THETA = 500000.0
EPS = 1e-6
RING = 4
LEAD = 3
LEVELS = 7
MASKED = -1e38
NORM_MEM, NORM_MIX, NORM_FFN = 0, 2 * KT, 4 * KT
LB_ROW = 6 * KT
QN_ROW = LB_ROW + 2 * HEADS_B
KN_ROW = QN_ROW + 2
ROWS = KN_ROW + 2


class Turns:

    def __init__(self, engine, sems):
        self.engine, self.sems, self.count, self.at = engine, sems, {}, None

    def value(self, key, less=0):
        c = self.count.get(key, 0) - less
        if self.at is None or not self.at[2].get(key):
            return c
        i, start, per = self.at
        return i * per[key] + (c - start * per[key])

    def any(self, key, less=0):
        return self.count.get(key, 0) - less > 0

    def move(self, key, n=1):
        self.count[key] = self.count.get(key, 0) + n

    def next(self, key, n=1):
        self.move(key, n)
        return self.value(key)

    def filled(self, b):
        self.move(f"free{b}")
        return self.next(f"full{b}")

    def skip(self, *banks):
        for b in banks:
            self.move(f"full{b}")
            self.move(f"free{b}")

    @contextmanager
    def loop(self, start, end, per):
        before = dict(self.count)
        with self.engine.Fori(start, end) as i:
            self.at = (i, start, per)
            yield i
            self.at = None
        moved = {k: c - before.get(k, 0) for k, c in self.count.items() if c != before.get(k, 0)}
        assert moved == per, (self.engine, moved, per)
        for k, n in per.items():
            self.count[k] += (end - start - 1) * n


def advance(steps_of_mixer, positions, i):
    for _ in range(positions.count(i)):
        next(steps_of_mixer, None)


def chain(*mixers):
    for n, mixer in enumerate(mixers):
        if n:
            yield
        yield from mixer


def short_parts(value, bits=11):
    parts, rest = [], float(value)
    for _ in range(4):
        scale = 2.0 ** (bits - 1 - np.floor(np.log2(abs(rest))))
        part = np.round(rest * scale) / scale
        parts.append(float(part))
        rest -= part
        if abs(rest) < 1e-30:
            break
    return parts


def trunk(nc, x, mem, positions, norm_mix, norm_ffn, norm_mem, w_in_a, q_norm_a, k_norm_a, sinks_a,
          w_in_b, lb_logits, g_norm_b, w_mem_kv, q_norm_m, k_norm_m, w_o, w_gate_up, w_down, out):
    ctx = ExitStack()
    with ctx:
        place = [nc.sbuf_base]

        def at(name, shape, dtype, offset):
            t = nc.alloc_sbuf_tensor_at(name, [P] + shape, dtype, offset=offset)
            return t

        def keep(name, shape, dtype=F32):
            size = int(np.prod(shape)) * 4
            place[0] = -(-place[0] // 32) * 32
            t = at(name, shape, dtype, place[0])
            place[0] += size
            return t

        x_tok = keep("x_tok", [TILES, D])
        hT = (keep("hT_hi", [KT, SEQ], F32R), keep("hT_lo", [KT, SEQ], F32R))
        raw = keep("raw", [RING, 2, COLS])
        w_hi = keep("w_hi", [RING, 2, COLS], F32R)
        w_lo = keep("w_lo", [RING, 2, COLS], F32R)
        kmT_b = keep("kmT_b", [4, N_MEM])
        vm_b = keep("vm_b", [TILES, COLS])
        tanh_ff = keep("tanh_ff", [TILES, COLS])
        act_ff = keep("act_ff", [TILES, COLS])
        squares = keep("squares", [COLS])
        ident = keep("ident", [P])
        level_mask = keep("level_mask", [LEVELS, P // 2])
        columns = keep("columns", [ROWS])
        q_gain = keep("q_gain", [HD_A])
        k_gain = keep("k_gain", [HD_A])
        g_gain = keep("g_gain", [HD_B])
        sink = keep("sink", [KV_A * GROUP_A])
        minus_sink = keep("minus_sink", [KV_A * GROUP_A])
        pos_int = keep("pos_int", [TILES], I32)
        cos = keep("cos", [TILES, ROT])
        sin = keep("sin", [TILES, ROT])
        ang = keep("ang", [TILES, ROT])
        turn = keep("turn", [TILES, ROT])
        freq = keep("freq", [ROT])
        lb_work = keep("lb_work", [4, HEADS_B])
        decay_table = keep("decay_table", [3, HEADS_B])
        decay_now = keep("decay_now", [3, 4])
        sum_sq = keep("sum_sq", [TILES, BLOCKS])
        sum_two = keep("sum_two", [TILES, 2])
        mem_sum_sq = keep("mem_sum_sq", [TILES, BLOCKS])
        mean_sq = keep("mean_sq", [TILES])
        rs = keep("rs", [TILES])
        half_rs = keep("half_rs", [TILES])
        half_rs2 = keep("half_rs2", [TILES])
        rs_mem = keep("rs_mem", [TILES])
        head_ss = keep("head_ss", [2 * GROUP_A])
        head_ms = keep("head_ms", [2 * GROUP_A])
        head_rs = keep("head_rs", [2 * GROUP_A])
        minus_half = keep("minus_half", [2 * GROUP_A])
        top = keep("top", [TILES, GROUP_A])
        minus_max = keep("minus_max", [TILES, GROUP_A])
        sink_less = keep("sink_less", [TILES, GROUP_A])
        exp_sink = keep("exp_sink", [TILES, GROUP_A])
        row_sum = keep("row_sum", [TILES, GROUP_A])
        denom = keep("denom", [TILES, GROUP_A])
        inv = keep("inv", [TILES, GROUP_A])

        arena = -(-place[0] // 32) * 32
        assert arena + 2 * FT * SEQ * 4 <= nc.sbuf_usable_end, (arena, nc.sbuf_usable_end)
        gT = (at("gT_hi", [FT, SEQ], F32R, arena), at("gT_lo", [FT, SEQ], F32R, arena + FT * SEQ * 4))

        def arena_map(begin, end):
            here = [arena + begin]

            def take(name, shape, dtype=F32):
                t = at(name, shape, dtype, here[0])
                here[0] += -(-int(np.prod(shape)) * 4 // 32) * 32
                assert here[0] <= arena + end, name
                return t
            return take

        half = KT * SEQ * 4
        take = arena_map(0, 2 * FT * SEQ * 4)
        memT = [(take(f"memT{n}_hi", [KT, SEQ], F32R), take(f"memT{n}_lo", [KT, SEQ], F32R)) for n in range(2)]
        mem_tok = take("mem_tok", [TILES, D])
        first_rows, rows = (at(name, [P], F32, arena + 2 * FT * SEQ * 4 - 2 * TILES * COLS * 4 + n * P * 4)
                            for n, name in enumerate(("first_rows", "rows")))
        kmT_a = take("kmT_a", [4, N_MEM])
        vm_a = take("vm_a", [TILES, COLS])
        kmT, vm = (kmT_a, kmT_b), (vm_a, vm_b)
        take = arena_map(0, 2 * half)
        mixT = (take("mixT_hi", [KT, SEQ], F32R), take("mixT_lo", [KT, SEQ], F32R))
        take = arena_map(2 * half, 2 * half + 3 * half)
        q_a = take("q_a", [TILES, COLS])
        sq_a = take("sq_a", [TILES, COLS])
        qm_a = take("qm_a", [TILES, COLS])
        kv_a = take("kv_a", [TILES, 6 * HD_A])
        k_twice = take("k_twice", [TILES, KV_A, 2, HD_A])
        kT = take("kT", [KV_A, SEQ])
        v_mid = take("v_mid", [KV_A * HD_A])
        qT_a = take("qT_a", [4, SEQ])
        p_a = take("p_a", [8 * P])
        pT_a = take("pT_a", [8, P])
        mix_a = take("mix_a", [TILES, COLS])
        masked_row = take("masked_row", [4, P // 2], F32R)
        ones_row = take("ones_row", [P // 2], F32R)
        mask_values = take("mask_values", [4, P // 2])
        rot = take("rot", [4, 2 * GROUP_A * ROT])
        take = arena_map(2 * half, 2 * FT * SEQ * 4)
        q_b = take("q_b", [TILES, COLS])
        z_b = take("z_b", [TILES, COLS])
        v_b = take("v_b", [TILES, COLS])
        gate_b = take("gate_b", [TILES, COLS])
        sq_b = take("sq_b", [TILES, COLS])
        tanh_q = take("tanh_q", [4, SEQ])
        tanh_z = take("tanh_z", [4, SEQ])
        query = take("query", [4, SEQ])
        decay = take("decay", [4, SEQ])
        key = take("key", [4, SEQ])
        query_in = take("query_in", [4, SEQ])
        block_decay = [decay] + [take(f"block_decay{n}", [4 * SEQ >> n]) for n in range(1, LEVELS)]
        wT = take("wT", [TILES, 4, P])
        wT_cross = take("wT_cross", [4, P])
        take = arena_map(2 * half + 7 * TILES * COLS * 4, 2 * FT * SEQ * 4)
        qT_b = take("qT_b", [4, SEQ])
        p_b = take("p_b", [8 * P])
        pT_b = take("pT_b", [8, P])
        qm_b = take("qm_b", [TILES, COLS])
        out_b = tanh_q

        out_tok = out_b[:, :, :].rearrange("p a b -> p (a b)").rearrange("p (t c) -> p t c", t=TILES)

        unit_bank = [ctx.enter_context(nc.psum_tensor(f"unit_bank{n}", [P, COLS], F32)) for n in range(4)]
        mix_bank = [ctx.enter_context(nc.psum_tensor(f"mix_bank{n}", [P, COLS], F32)) for n in range(4)]

        names = (
            [f"arrived{s}" for s in range(RING)]
            + [f"mem_in{c}" for c in range(BLOCKS)] + [f"x_in{c}" for c in range(BLOCKS)]
            + ["first_rows_in", "rows_in", "tables_in", "stored"]
            + ["hi_ready", "lo_ready", "piece_used"]
            + ["unit_free0", "unit_free1"]
            + [f"full{b}" for b in range(4)] + [f"free{b}" for b in range(4)]
            + ["gained", "hi_block"]
            + ["ident_ready", "freq_ready", "mask_rows_ready", "mem_squares", "x_squares",
               "rs_ready", "mem_rs_ready"]
            + ["sq_ready", "ss_ready", "head_rs_ready", "heads_ready"]
            + ["minus_max_ready", "angles_ready", "sines_ready", "lb_less_max", "lb_exp"]
            + ["tanh_ff_ready", "tanh_q_ready", "tanh_gate_ready", "gate_used", "rung_ready"]
            + ["dve_chain", "pool_chain"])
        sems = {n: ctx.enter_context(nc.semaphore(n)) for n in names}
        sems["split"] = sems["at"] = sems["piece_used"]
        block = ctx.enter_context(nc.Block())

        GATE_PARTS = [n * TOKEN_WIDTH for n in range(4)]
        MIXED_KTS = [[12, 14, 0, 2], [4, 6], [8, 10]]
        ALL_KTS = list(range(0, KT, 2))
        FF_KTS = list(range(0, FT, 2))
        HEAD_STEPS = [4, 5, 7]
        TAIL_STEPS = [0, 2, 3, 5]
        LAST_TAIL_STEPS = [8, 9, 10, 11]
        NORM_STEPS = [0, 1, 2, 3]
        MEMORY_STEPS = [3, 5, 7, 8, 11, 12, 14]
        REC_HEAD_STEPS = [18, 20, 22, 24, 26, 28, 30]
        REC_TAIL_STEPS = [0, 2, 4, 6, 11]
        REC_NORM_TAIL_STEPS = [0, 2, 4, 7, 8, 10, 11]
        SPLIT_LEVEL = 5

        @block.sync
        def _(sp):
            t = Turns(sp, sems)
            slot = [0]

            def piece(w, kt, col):
                s = slot[0] % RING
                slot[0] += 1
                t.move("lo_ready")
                if t.any("lo_ready", RING):
                    sp.wait_ge(sems["lo_ready"], t.value("lo_ready", RING))
                sp.dma_start(raw[:, s, :, :], w[kt * P:(kt + 2) * P, bass.ds(col, COLS)]
                             .rearrange("(j p) n -> p j n", p=P)).then_inc(sems[f"arrived{s}"], 16)

            def unit(w, col, kts=ALL_KTS):
                for kt in kts:
                    piece(w, kt, col)

            mem_rows = mem.rearrange("b (t p) d -> p (b t) d", p=P)
            x_rows = x.rearrange("b (t p) d -> p (b t) d", p=P)

            def mem_block(c):
                cols = slice(c * COLS, (c + 1) * COLS)
                sp.dma_start(mem_tok[:, :, cols], mem_rows[:, :, cols]).then_inc(sems[f"mem_in{c}"], 16)

            mem_block(0)
            sp.dma_start(first_rows[0:2 * KT, :],
                         norm_mem.rearrange("l (t p) -> (l t) p", p=P)).then_inc(sems["first_rows_in"], 16)
            w_kv = [w_mem_kv[n, :, :] for n in range(2)]
            piece(w_kv[0], 0, 0)
            for c in range(1, BLOCKS):
                piece(w_kv[0], 2 * c, 0)
                mem_block(c)
            r = 0
            for src in (norm_mix.rearrange("l (t p) -> (l t) p", p=P),
                        norm_ffn.rearrange("l (t p) -> (l t) p", p=P),
                        lb_logits.rearrange("l (t p) -> (l t) p", p=P), q_norm_m, k_norm_m):
                sp.dma_start(rows[r:r + src.shape[0], :], src).then_inc(sems["rows_in"], 16)
                r += src.shape[0]
            assert NORM_MIX + r == ROWS
            for dst, src in ((q_gain, q_norm_a), (k_gain, k_norm_a), (g_gain, g_norm_b), (sink, sinks_a)):
                sp.dma_start(dst[:, :], src[0, :].partition_broadcast(P)).then_inc(sems["tables_in"], 16)
            sp.dma_start(pos_int[:, :], positions.rearrange("b (t p) -> p (b t)", p=P),
                         allow_slow_non_contiguous=True
                         ).then_inc(sems["tables_in"], 16)
            unit(w_kv[0], 0, ALL_KTS[BLOCKS:])
            for c in range(BLOCKS):
                cols = slice(c * COLS, (c + 1) * COLS)
                sp.dma_start(x_tok[:, :, cols], x_rows[:, :, cols]).then_inc(sems[f"x_in{c}"], 16)
            unit(w_kv[0], COLS)
            unit(w_kv[1], 0)
            unit(w_kv[1], COLS)

            def projection_ffn(layer):
                wo = w_o[layer, :, :]
                for kts in MIXED_KTS:
                    unit(wo, 0, kts)
                    unit(wo, COLS, kts)
                unit(wo, 2 * COLS)
                unit(wo, 3 * COLS)
                wg = w_gate_up[layer, :, :]
                unit(wg, 0)
                unit(wg, D_FF)
                with t.loop(1, CHUNKS_FF, {"lo_ready": KT}) as j:
                    unit(wg, j * COLS)
                    unit(wg, j * COLS + D_FF)
                wd = w_down[layer, :, :]
                for c in range(BLOCKS):
                    unit(wd, c * COLS, FF_KTS)

            wa = w_in_a[0, :, :]
            unit(wa, TOKEN_WIDTH)
            unit(wa, TOKEN_WIDTH + 2 * KV_A * HD_A)
            for g in range(GROUPS):
                unit(wa, g * COLS)
            projection_ffn(0)

            wb = w_in_b[0, :, :]
            unit(wb, 4 * TOKEN_WIDTH)
            for part in GATE_PARTS:
                unit(wb, part)
            with t.loop(1, GROUPS, {"lo_ready": 2 * KT}) as g:
                for part in GATE_PARTS:
                    unit(wb, g * COLS + part)
            projection_ffn(1)

        @block.gpsimd
        def _(pool):
            t = Turns(pool, sems)

            pool.memset(ident[:, :], 0.0).then_inc(sems["pool_chain"], 1)
            pool.wait_ge(sems["pool_chain"], t.next("pool_chain"))
            pool.affine_select(out=ident[:, :], in_=ident[:, :], compare_op=ALU.not_equal, fill=1.0,
                               base=0, pattern=[[-1, P]], channel_multiplier=1).then_inc(sems["ident_ready"], 1)
            pool.memset(minus_half[:, :], -0.5).then_inc(sems["pool_chain"], 1)
            pool.wait_ge(sems["pool_chain"], t.next("pool_chain"))

            def token_rs(squares_key, src, dst, ready):
                pool.wait_ge(sems[squares_key], t.next(squares_key, TILES * BLOCKS))
                pool.tensor_tensor(sum_two[:, :, :], src[:, :, 0:2], src[:, :, 2:4], ALU.add).then_inc(sems["pool_chain"], 1)
                pool.wait_ge(sems["pool_chain"], t.next("pool_chain"))
                pool.tensor_tensor(mean_sq[:, :], sum_two[:, :, 0], sum_two[:, :, 1], ALU.add).then_inc(sems["pool_chain"], 1)
                pool.wait_ge(sems["pool_chain"], t.next("pool_chain"))
                pool.tensor_scalar(mean_sq[:, :], mean_sq[:, :], 1.0 / D, EPS, ALU.mult, ALU.add).then_inc(sems["pool_chain"], 1)
                pool.wait_ge(sems["pool_chain"], t.next("pool_chain"))
                pool.tensor_tensor(dst[:, :], mean_sq[:, :], minus_half[:, 0:TILES], ALU.pow).then_inc(sems["pool_chain"], 1)
                pool.wait_ge(sems["pool_chain"], t.next("pool_chain"))
                pool.tensor_scalar(half_rs[:, :], dst[:, :], 0.5, 0.0, ALU.mult, ALU.add).then_inc(sems["pool_chain"], 1)
                pool.wait_ge(sems["pool_chain"], t.next("pool_chain"))
                pool.tensor_tensor(half_rs2[:, :], half_rs[:, :], dst[:, :], ALU.mult).then_inc(sems[ready], 1)

            def heads(n, width):
                pool.wait_ge(sems["ss_ready"], t.next("ss_ready"))
                pool.tensor_scalar(head_ms[:, 0:n], head_ss[:, 0:n], 1.0 / width, EPS, ALU.mult, ALU.add).then_inc(sems["pool_chain"], 1)
                pool.wait_ge(sems["pool_chain"], t.next("pool_chain"))
                pool.tensor_tensor(head_rs[:, 0:n], head_ms[:, 0:n], minus_half[:, 0:n],
                                   ALU.pow).then_inc(sems["head_rs_ready"], 1)

            token_rs("mem_squares", mem_sum_sq, rs_mem, "mem_rs_ready")
            pool.memset(level_mask[:, :, :], 1.0).then_inc(sems["pool_chain"], 1)
            pool.wait_ge(sems["pool_chain"], t.next("pool_chain"))
            for n in range(1, LEVELS + 1):
                size, blocks = 1 << n, P >> n
                m = level_mask[:, n - 1, :].rearrange("p (b o) -> p b o", o=size // 2)
                pool.affine_select(out=m, in_=m, compare_op=ALU.is_ge, fill=0.0, base=0,
                                   pattern=[[-size, blocks], [0, size // 2]], channel_multiplier=1).then_inc(sems["pool_chain"], 1)
                pool.wait_ge(sems["pool_chain"], t.next("pool_chain"))
                pool.affine_select(out=m, in_=m, compare_op=ALU.is_ge, fill=0.0, base=size // 2 - 1,
                                   pattern=[[size, blocks], [0, size // 2]], channel_multiplier=-1).then_inc(sems["pool_chain"], 1)
                pool.wait_ge(sems["pool_chain"], t.next("pool_chain"))
            for i in range(ROT):
                ins = pool.memset(freq[:, i:i + 1], float(np.float32(THETA) ** np.float32(-i / ROT)))
            ins.then_inc(sems["freq_ready"], 1)
            heads(8, P)
            token_rs("x_squares", sum_sq, rs, "rs_ready")
            heads(8, P)
            pool.memset(mask_values[:, :, :], 1.0).then_inc(sems["pool_chain"], 1)
            pool.wait_ge(sems["pool_chain"], t.next("pool_chain"))
            pool.tensor_scalar(ones_row[:, :], mask_values[:, 0, :], 1.0, 0.0, ALU.mult, ALU.add)
            pool.tensor_scalar(masked_row[:, :, :], mask_values[:, :, :], MASKED, 0.0, ALU.mult,
                               ALU.add).then_inc(sems["mask_rows_ready"], 1)
            heads(2 * KV_A, HD_A)
            heads(8, P)
            for g in range(GROUPS):
                heads(2 * GROUP_A, HD_A)
            token_rs("x_squares", sum_sq, rs, "rs_ready")
            token_rs("x_squares", sum_sq, rs, "rs_ready")
            heads(8, P)
            for g in range(GROUPS):
                heads(8, P)
            token_rs("x_squares", sum_sq, rs, "rs_ready")

        @block.scalar
        def _(act):
            t = Turns(act, sems)
            slot = [0]

            def split():
                s = slot[0] % RING
                slot[0] += 1
                act.wait_ge(sems[f"arrived{s}"], t.next(f"arrived{s}", 16))
                t.move("split")
                if t.any("split", RING):
                    act.wait_ge(sems["piece_used"], t.value("split", RING))
                act.activation(w_hi[:, s, :, :], raw[:, s, :, :], ACT.Copy).then_inc(sems["hi_ready"], 1)

            def pieces(n, tail=False):
                for i in range(n):
                    yield i
                    if not tail or i + LEAD < n:
                        split()
                    t.move("at")

            def unit_done(pair):
                t.move(f"unit_free{pair}", TILES)
                return t.value("at")

            def heads_4(bank):
                return bank[:, :].rearrange("p (h n) -> p h n", h=4)

            def to_tok(dst, pair, scale=None, cols=COLS, sq=None, sq_cols=COLS):
                scale = rs if scale is None else scale
                act.wait_ge(sems["piece_used"], unit_done(pair))
                for s in range(TILES):
                    act.activation(dst[:, s, 0:cols], unit_bank[2 * pair + s][:, 0:cols], ACT.Copy,
                                   scale=scale[:, s:s + 1]).then_inc(sems[f"unit_free{pair}"], 1)
                if sq is not None:
                    act.wait_ge(sems[f"unit_free{pair}"], t.value(f"unit_free{pair}"))
                    act.activation(sq[:, :, 0:sq_cols], dst[:, :, 0:sq_cols], ACT.Square).then_inc(sems["sq_ready"], 1)

            def gained_block(dst, kt):
                for s in range(TILES):
                    t.skip(s)
                    act.wait_ge(sems["gained"], t.next("gained"))
                    act.activation(dst[0][:, bass.ds(kt, 4), s * P:(s + 1) * P],
                                   act_ff[:, s, :].rearrange("p (k n) -> p k n", k=4),
                                   ACT.Copy).then_inc(sems["hi_block"], 1)

            def plain_block(dst, kt):
                for s in range(TILES):
                    act.wait_ge(sems[f"full{s}"], t.filled(s))
                    act.activation(dst[0][:, bass.ds(kt, 4), s * P:(s + 1) * P], heads_4(mix_bank[s]),
                                   ACT.Copy).then_inc(sems["hi_block"], 1)

            def square_sums(src, dst, block, ready):
                for s in range(TILES):
                    if t.any(ready):
                        act.wait_ge(sems[ready], t.value(ready))
                    t.move(ready)
                    act.activation(squares[:, :], src[:, s, bass.ds(block * COLS, COLS)], ACT.Square,
                                   accum_out=dst[:, s, bass.ds(block, 1)]).then_inc(sems[ready], 1)

            def turn_heads(dst, gain=None, count=4):
                for s in range(TILES):
                    act.wait_ge(sems[f"full{s}"], t.filled(s))
                    act.activation(dst[:, 0:count, s * P:(s + 1) * P], heads_4(mix_bank[s])[:, 0:count, :], ACT.Copy,
                                   scale=1.0 if gain is None else gain).then_inc(sems[f"free{s}"], 1)

            def exps(s, window, probs):
                n_heads, scale = (GROUP_A, HD_A ** -0.5) if window else (4, P ** -0.5)
                keys = 8 * P // n_heads
                act.wait_ge(sems["full2"], t.filled(2))
                act.wait_ge(sems["full3"], t.filled(3))
                act.wait_ge(sems["minus_max_ready"], t.next("minus_max_ready"))
                if window:
                    act.activation(exp_sink[:, s, :], sink_less[:, s, :], ACT.Exp)
                for h in range(n_heads):
                    b, o = 2 + h % 2, h // 2 * keys
                    ins = act.activation(probs[:, h * keys:(h + 1) * keys], mix_bank[b][:, o:o + keys], ACT.Exp,
                                         bias=minus_max[:, s, h:h + 1], scale=scale,
                                         accum_out=row_sum[:, s, h:h + 1])
                    if h >= n_heads - 2:
                        ins.then_inc(sems[f"free{b}"], 1)

            def turn_probs(dst):
                act.wait_ge(sems["full0"], t.filled(0))
                act.activation(dst[:, 0:4, :], heads_4(mix_bank[0]), ACT.Copy).then_inc(sems["free0"], 1)
                act.wait_ge(sems["full1"], t.filled(1))

            def attention_head(window, qT, probs, pT, gain=None):
                turn_heads(qT, gain)
                yield
                exps(0, window, probs)
                yield
                turn_probs(pT)

            def attention_tail(window, probs, pT, kt):
                exps(1, window, probs)
                t.skip(0)
                yield
                turn_probs(pT)
                yield
                t.skip(0)
                yield
                plain_block(mixT, kt)

            def rec_start():
                for s in range(TILES):
                    act.wait_ge(sems[f"full{s}"], t.filled(s))
                    act.activation(tanh_q[:, :, s * P:(s + 1) * P], heads_4(mix_bank[s]),
                                   ACT.Tanh, scale=0.5).then_inc(sems["tanh_q_ready"], 1)
                for s in range(TILES):
                    act.wait_ge(sems[f"full{2 + s}"], t.filled(2 + s))
                    act.activation(tanh_z[:, :, s * P:(s + 1) * P], heads_4(mix_bank[2 + s]),
                                   ACT.Tanh, scale=0.5).then_inc(sems[f"free{2 + s}"], 1)

            def rec_cross():
                act.wait_ge(sems["full0"], t.filled(0))
                act.activation(wT_cross[:, :, :], heads_4(mix_bank[0]), ACT.Copy).then_inc(sems["free0"], 1)

            def rec_out():
                for s in range(TILES):
                    act.wait_ge(sems[f"full{1 + s}"], t.filled(1 + s))
                    act.activation(out_tok[:, s, :], mix_bank[1 + s][:, :], ACT.Copy,
                                   scale=0.5).then_inc(sems[f"free{1 + s}"], 1)
                act.wait_ge(sems["free1"], t.value("free1"))
                act.wait_ge(sems["free2"], t.value("free2"))
                act.activation(sq_b[:, :, :], out_tok, ACT.Square).then_inc(sems["sq_ready"], 1)

            def recurrence_head():
                rec_start()
                yield
                t.skip(0, 1)
                for n in range(1, SPLIT_LEVEL + 1):
                    yield
                    t.skip(*((2, 3) if n % 2 else (0, 1)))

            def recurrence_tail(kt):
                for n in range(SPLIT_LEVEL + 1, LEVELS + 1):
                    t.skip(*((2, 3) if n % 2 else (0, 1)))
                    yield
                rec_cross()
                yield
                rec_out()
                yield
                plain_block(mixT, kt)

            def gate_unit(pair):
                act.wait_ge(sems["piece_used"], unit_done(pair))
                if t.any("gate_used"):
                    act.wait_ge(sems["gate_used"], t.value("gate_used"))
                for s in range(TILES):
                    act.activation(gate_b[:, s, :], unit_bank[2 * pair + s][:, :], ACT.Tanh,
                                   scale=half_rs[:, s:s + 1]).then_inc(sems["tanh_gate_ready"], 1)
                t.move("gate_used")

            t.skip(3)
            t.skip(3)
            split()
            gained_block(memT[0], 0)
            for _ in range(LEAD - 1):
                split()
            for i in pieces(8):
                if i in (1, 2, 4):
                    gained_block(memT[0], (1, 2, 4).index(i) * 4 + 4)
                if i in (3, 5, 6, 7):
                    c = (3, 5, 6, 7).index(i)
                    act.wait_ge(sems[f"mem_in{c}"], t.next(f"mem_in{c}", 16))
                    square_sums(mem_tok, mem_sum_sq, c, "mem_squares")
            act.wait_ge(sems["mem_rs_ready"], t.next("mem_rs_ready"))
            to_tok(tanh_ff, 0, rs_mem, sq=vm_b)

            def lb_exps():
                act.wait_ge(sems["lb_less_max"], t.next("lb_less_max"))
                act.activation(lb_work[:, 0:2, :], lb_work[:, 0:2, :], ACT.Exp).then_inc(sems["lb_exp"], 1)

            def sines():
                act.wait_ge(sems["angles_ready"], t.next("angles_ready"))
                act.activation(sin[:, :, :], ang[:, :, :], ACT.Sin)
                act.activation(turn[:, :, :], ang[:, :, :], ACT.Sin, scale=0.5).then_inc(sems["sines_ready"], 1)

            for i in pieces(8):
                if i % 2 == 0:
                    gained_block(memT[1], i * 2)
                if i == 6:
                    lb_exps()
                if i == 7:
                    turn_heads(kmT[0], columns[:, KN_ROW:KN_ROW + 1])
            to_tok(vm[0], 1, rs_mem)
            for i in pieces(8):
                if i % 2 == 0:
                    gained_block(hT, i * 2)
                    act.wait_ge(sems[f"x_in{i // 2}"], t.next(f"x_in{i // 2}", 16))
                    square_sums(x_tok, sum_sq, i // 2, "x_squares")
            to_tok(tanh_ff, 0, rs_mem, sq=vm_b)
            for i in pieces(8):
                if i == 4:
                    turn_heads(kmT[1], columns[:, KN_ROW + 1:KN_ROW + 2])
            to_tok(vm[1], 1, rs_mem)
            sines()

            def x_sums(pair, block):
                act.wait_ge(sems["piece_used"], unit_done(pair))
                act.wait_ge(sems[f"unit_free{pair}"], t.value(f"unit_free{pair}"))
                square_sums(x_tok, sum_sq, block, "x_squares")

            def projection_ffn(layer, mix, pair):
                other = 1 - pair
                for i in pieces(16):
                    if i == 14:
                        x_sums(pair, 0)
                    mix(i)
                x_sums(other, 1)
                for i in pieces(8):
                    if i in (1, 4):
                        gained_block(hT, (1, 4).index(i) * 4)
                x_sums(pair, 2)
                for i in pieces(8):
                    if i == 1:
                        gained_block(hT, 8)
                x_sums(other, 3)

                def chunk(j):
                    for i in pieces(8):
                        if j is None and i == 2:
                            gained_block(hT, 12)
                        if j is not None and i == 1:
                            plain_block(gT, (j - 1) * 4)
                    if j is None:
                        act.wait_ge(sems["rs_ready"], t.next("rs_ready"))
                    act.wait_ge(sems["piece_used"], unit_done(pair))
                    act.wait_ge(sems[f"unit_free{other}"], t.value(f"unit_free{other}"))
                    for s in range(TILES):
                        act.activation(tanh_ff[:, s, :], unit_bank[2 * pair + s][:, :], ACT.Tanh,
                                       scale=half_rs[:, s:s + 1]).then_inc(sems["tanh_ff_ready"], 1)
                    for i in pieces(8):
                        pass
                    act.wait_ge(sems["piece_used"], unit_done(other))

                chunk(None)
                with t.loop(1, CHUNKS_FF, per_chunk) as j:
                    chunk(j)

                def store(pair, c):
                    act.wait_ge(sems["piece_used"], unit_done(pair))
                    act.wait_ge(sems[f"unit_free{pair}"], t.value(f"unit_free{pair}"))
                    act.dma_start(out.rearrange("b (t p) d -> p (b t) d", p=P)[:, :, c * COLS:(c + 1) * COLS],
                                  x_tok[:, :, c * COLS:(c + 1) * COLS]).then_inc(sems["stored"], 16)

                for c in range(BLOCKS):
                    for i in pieces(len(FF_KTS), tail=layer == 1 and c == BLOCKS - 1):
                        if c == 0 and i == 1:
                            plain_block(gT, FT - 4)
                        if layer == 0 and c > 0 and i == 2:
                            gained_block(hT, (c - 1) * 4)
                    if layer == 0:
                        x_sums((pair, other)[c % 2], c)
                    else:
                        store((pair, other)[c % 2], c)
                if layer == 1:
                    act.wait_ge(sems["stored"], 16 * BLOCKS)

            def slots(n):
                return {f"arrived{s}": 16 * n // RING for s in range(RING)} | {"split": n, "at": n}

            def banks(*counts):
                return {f"{k}{b}": n for b, n in enumerate(counts) if n for k in ("full", "free")}

            per_chunk = slots(16) | banks(1, 1) | {"unit_free0": 2, "unit_free1": 2}

            act.wait_ge(sems["rs_ready"], t.next("rs_ready"))
            for i in pieces(8):
                pass
            to_tok(kv_a, 0, cols=2 * KV_A * HD_A, sq=sq_a, sq_cols=KV_A * HD_A)
            for i in pieces(8):
                if i == 4:
                    turn_heads(kT, count=KV_A)
            to_tok(qm_a, 1, sq=sq_a)
            def window_tail_then_head(tail, head, i):
                advance(tail, TAIL_STEPS, i)
                advance(head, HEAD_STEPS, i)

            head = attention_head(False, qT_a, p_a, pT_a, columns[:, QN_ROW:QN_ROW + 1])
            for i in pieces(8):
                advance(head, HEAD_STEPS, i)
            to_tok(q_a, 0, sq=sq_a)
            for g in range(1, GROUPS):
                tail = attention_tail(g > 1, p_a, pT_a, (g - 2) % 4 * 4)
                head = attention_head(True, qT_a, p_a, pT_a)
                for i in pieces(8):
                    window_tail_then_head(tail, head, i)
                to_tok(q_a, g % 2, sq=sq_a)
            tails, head = [attention_tail(True, p_a, pT_a, g * 4) for g in (1, 2)], attention_head(True, qT_a, p_a, pT_a)

            def last_windows(i):
                window_tail_then_head(tails[0], head, i)
                advance(tails[1], LAST_TAIL_STEPS, i)

            projection_ffn(0, last_windows, 1)

            def group_b(before, positions):
                head = recurrence_head()
                for i in pieces(8):
                    advance(before, positions, i)
                to_tok(q_b, 0)
                for i in pieces(8):
                    advance(before, positions, 8 + i)
                to_tok(z_b, 1)
                for i in pieces(8):
                    advance(head, REC_HEAD_STEPS, 16 + i)
                to_tok(v_b, 0)
                for i in pieces(8):
                    advance(head, REC_HEAD_STEPS, 24 + i)
                gate_unit(1)

            for i in pieces(8):
                if i == 2:
                    gained_block(hT, 12)
            act.wait_ge(sems["rs_ready"], t.next("rs_ready"))
            to_tok(qm_b, 1, sq=sq_b)
            group_b(chain(attention_head(False, qT_b, p_b, pT_b, columns[:, QN_ROW + 1:QN_ROW + 2]),
                          attention_tail(False, p_b, pT_b, 12)), MEMORY_STEPS)
            with t.loop(1, GROUPS, slots(32) | banks(7, 7, 6, 5)
                        | {"unit_free0": 4, "unit_free1": 4, "gate_used": 1}) as g:
                group_b(recurrence_tail((g - 1) * 4), REC_TAIL_STEPS)
            tail = recurrence_tail(8)
            projection_ffn(1, lambda i: advance(tail, REC_TAIL_STEPS, i), 0)

        @block.vector
        def _(dve):
            t = Turns(dve, sems)
            slot = [0]

            def split():
                s = slot[0] % RING
                slot[0] += 1
                dve.wait_ge(sems["hi_ready"], t.next("hi_ready"))
                t.move("split")
                if t.any("split", RING):
                    dve.wait_ge(sems["piece_used"], t.value("split", RING))
                dve.tensor_tensor(w_lo[:, s, :, :], raw[:, s, :, :], w_hi[:, s, :, :].bitcast(F32),
                                  ALU.subtract).then_inc(sems["lo_ready"], 1)

            def pieces(n, tail=False):
                for i in range(n):
                    yield i
                    if not tail or i + LEAD < n:
                        split()
                    t.move("at")

            def unit_done(pair):
                t.move(f"unit_free{pair}", TILES)
                return t.value("at")

            def pass_unit(pair):
                t.move(f"unit_free{pair}", TILES)

            def heads_4(bank):
                return bank[:, :].rearrange("p (h n) -> p h n", h=4)

            def gained_block(dst, kt, row):
                for s in range(TILES):
                    dve.wait_ge(sems[f"full{s}"], t.filled(s))
                    dve.tensor_tensor(act_ff[:, s, :].rearrange("p (k n) -> p k n", k=4), heads_4(mix_bank[s]),
                                      columns[:, bass.ds(row + kt, 4)].unsqueeze(2).broadcast_to([P, 4, P]),
                                      ALU.mult).then_inc(sems["gained"], 1)
                for s in range(TILES):
                    dve.wait_ge(sems["hi_block"], t.next("hi_block"))
                    dve.tensor_tensor(dst[1][:, bass.ds(kt, 4), s * P:(s + 1) * P],
                                      act_ff[:, s, :].rearrange("p (k n) -> p k n", k=4),
                                      dst[0][:, bass.ds(kt, 4), s * P:(s + 1) * P].bitcast(F32),
                                      ALU.subtract).then_inc(sems[f"free{s}"], 1)

            def plain_block(dst, kt):
                for s in range(TILES):
                    t.skip(s)
                    dve.wait_ge(sems["hi_block"], t.next("hi_block"))
                    dve.tensor_tensor(dst[1][:, bass.ds(kt, 4), s * P:(s + 1) * P], heads_4(mix_bank[s]),
                                      dst[0][:, bass.ds(kt, 4), s * P:(s + 1) * P].bitcast(F32),
                                      ALU.subtract).then_inc(sems[f"free{s}"], 1)

            def head_sums(sq, out):
                dve.wait_ge(sems["sq_ready"], t.next("sq_ready"))
                dve.tensor_reduce(out, sq, AX.X, ALU.add).then_inc(sems["ss_ready"], 1)

            def norm_heads(tile, factors, shape, last):
                dve.wait_ge(sems["head_rs_ready"], t.next("head_rs_ready"))
                dve.tensor_tensor(tile, tile, factors.broadcast_to(shape), ALU.mult).then_inc(sems[last], 1)
                dve.wait_ge(sems[last], t.next(last))

            def norm_window_heads(tile, sq, gain, heads, last):
                tile, sq = (m[:, :, 0:heads * HD_A].rearrange("p t (h d) -> p t h d", d=HD_A) for m in (tile, sq))
                by_head = [m[:, 0:TILES * heads].rearrange("p (t h) -> p t h", t=TILES) for m in (head_ss, head_rs)]
                head_sums(sq, by_head[0])
                yield
                norm_heads(tile, by_head[1].unsqueeze(3), [P, TILES, heads, HD_A], "dve_chain")
                yield
                for s in range(TILES):
                    ins = dve.tensor_tensor(tile[:, s, :, :], tile[:, s, :, :],
                                            gain[:, :].unsqueeze(1).broadcast_to([P, heads, HD_A]), ALU.mult)
                ins.then_inc(sems["dve_chain"], 1)
                dve.wait_ge(sems["dve_chain"], t.next("dve_chain"))
                yield
                one, two = tile[:, :, :, 0:ROT], tile[:, :, :, ROT:2 * ROT]
                shape = [P, TILES, heads, ROT]
                c, z = (m[:, :, :].unsqueeze(2).broadcast_to(shape) for m in (cos, sin))
                parts = [rot[:, n, 0:TILES * heads * ROT].rearrange("p (t h r) -> p t h r", t=TILES, h=heads) for n in range(4)]
                for part, (a, b) in zip(parts, ((one, c), (two, z), (two, c), (one, z))):
                    ins = dve.tensor_tensor(part, a, b, ALU.mult)
                ins.then_inc(sems["dve_chain"], 1)
                dve.wait_ge(sems["dve_chain"], t.next("dve_chain"))
                dve.tensor_tensor(one, parts[0], parts[1], ALU.subtract)
                dve.tensor_tensor(two, parts[2], parts[3], ALU.add).then_inc(sems[last], 1)
                dve.wait_ge(sems[last], t.next(last))

            def norm_memory_heads(tile, sq):
                by_head = [m.rearrange("p t (h d) -> p (t h) d", h=4) for m in (tile[:, :, :], sq[:, :, :])]
                head_sums(by_head[1], head_ss[:, 0:8])
                yield
                norm_heads(by_head[0], head_rs[:, 0:8].unsqueeze(2), [P, 8, P], "heads_ready")

            def minus_tops(s, window, group=None):
                n_heads, scale = (GROUP_A, HD_A ** -0.5) if window else (4, P ** -0.5)
                keys = 8 * P // n_heads
                for b in (2, 3):
                    dve.wait_ge(sems[f"full{b}"], t.filled(b))
                    ins = dve.tensor_reduce(top[:, s, b - 2:n_heads:2],
                                            mix_bank[b][:, :].rearrange("p (h k) -> p h k", k=keys), AX.X, ALU.max)
                    ins.then_inc(sems["dve_chain"], 1)
                    dve.wait_ge(sems["dve_chain"], t.next("dve_chain"))
                if not window:
                    dve.tensor_scalar(minus_max[:, s, 0:n_heads], top[:, s, 0:n_heads], -scale, None,
                                      ALU.mult).then_inc(sems["minus_max_ready"], 1)
                    return
                dve.tensor_scalar(top[:, s, :], top[:, s, :], -scale, None, ALU.mult).then_inc(sems["dve_chain"], 1)
                dve.wait_ge(sems["dve_chain"], t.next("dve_chain"))
                dve.tensor_tensor(minus_max[:, s, :], top[:, s, :],
                                  minus_sink[:, group * GROUP_A:(group + 1) * GROUP_A], ALU.min).then_inc(sems["dve_chain"], 1)
                dve.wait_ge(sems["dve_chain"], t.next("dve_chain"))
                dve.tensor_tensor(sink_less[:, s, :], sink[:, group * GROUP_A:(group + 1) * GROUP_A], minus_max[:, s, :],
                                  ALU.add).then_inc(sems["minus_max_ready"], 1)

            def turn_probs(dst):
                t.skip(0)
                dve.wait_ge(sems["full1"], t.filled(1))
                dve.tensor_copy(dst[:, 4:8, :], heads_4(mix_bank[1])).then_inc(sems["free1"], 1)

            def values(s, window, mix):
                n_heads = GROUP_A if window else 4
                dve.wait_ge(sems["full0"], t.filled(0))
                total = row_sum[:, s, 0:n_heads]
                if window:
                    dve.tensor_tensor(denom[:, s, :], row_sum[:, s, :], exp_sink[:, s, :], ALU.add).then_inc(sems["dve_chain"], 1)
                    dve.wait_ge(sems["dve_chain"], t.next("dve_chain"))
                    total = denom[:, s, :]
                dve.reciprocal(inv[:, s, 0:n_heads], total).then_inc(sems["dve_chain"], 1)
                dve.wait_ge(sems["dve_chain"], t.next("dve_chain"))
                width = COLS // n_heads
                dve.tensor_tensor(mix[:, s, :].rearrange("p (h d) -> p h d", d=width),
                                  mix_bank[0][:, :].rearrange("p (h d) -> p h d", d=width),
                                  inv[:, s, 0:n_heads].unsqueeze(2).broadcast_to([P, n_heads, width]),
                                  ALU.mult).then_inc(sems["free0"], 1)

            def attention_head(window, pT, group=None):
                t.skip(0, 1)
                yield
                minus_tops(0, window, group)
                yield
                turn_probs(pT)
                minus_tops(1, window, group)

            def attention_tail(window, pT, mix, kt):
                values(0, window, mix)
                yield
                turn_probs(pT)
                yield
                values(1, window, mix)
                yield
                plain_block(mixT, kt)

            def flat(tile):
                return tile[:, :, :].rearrange("p h n -> p (h n)")

            def rec_start(g):
                dve.tensor_copy(decay_now[:, :, :], decay_table[:, :, bass.ds(g * 4, 4)]).then_inc(sems["dve_chain"], 1)
                dve.wait_ge(sems["dve_chain"], t.next("dve_chain"))
                for s in range(TILES):
                    dve.wait_ge(sems["tanh_q_ready"], t.next("tanh_q_ready"))
                    t.skip(s)
                    dve.scalar_tensor_tensor(out=query[:, :, s * P:(s + 1) * P], in0=tanh_q[:, :, s * P:(s + 1) * P],
                                             scalar=1.0, in1=heads_4(mix_bank[s]), op0=ALU.add,
                                             op1=ALU.mult).then_inc(sems[f"free{s}"], 1)
                t.skip(2, 3)
                dve.wait_ge(sems["free2"], t.value("free2"))
                dve.wait_ge(sems["free3"], t.value("free3"))
                for h in range(4):
                    dve.tensor_scalar(decay[:, h, :], tanh_z[:, h, :], decay_now[:, 0, h:h + 1],
                                      decay_now[:, 1, h:h + 1], ALU.mult, ALU.add)
                    ins = dve.tensor_scalar(key[:, h, :], tanh_z[:, h, :], decay_now[:, 2, h:h + 1],
                                            decay_now[:, 0, h:h + 1], ALU.mult, ALU.add)
                ins.then_inc(sems["dve_chain"], 1)
                dve.wait_ge(sems["dve_chain"], t.next("dve_chain"))
                dve.wait_ge(sems["free0"], t.value("free0"))
                dve.wait_ge(sems["free1"], t.value("free1"))
                dve.tensor_tensor(query_in[:, :, :], query[:, :, :], decay[:, :, :], ALU.mult).then_inc(sems["rung_ready"], 1)
                dve.wait_ge(sems["rung_ready"], t.next("rung_ready"))

            def rec_same():
                for s in range(TILES):
                    dve.wait_ge(sems[f"full{s}"], t.filled(s))
                    dve.tensor_tensor(wT[:, s, :, :], heads_4(mix_bank[s]), ident[:, :].unsqueeze(1).broadcast_to([P, 4, P]),
                                      ALU.mult).then_inc(sems[f"free{s}"], 1)

            def rec_level(n):
                banks = (2, 3) if n % 2 else (0, 1)
                for b in (0, 1) if n % 2 else (2, 3):
                    dve.wait_ge(sems[f"free{b}"], t.value(f"free{b}"))
                if n > 1:
                    dve.wait_ge(sems["rung_ready"], t.next("rung_ready"))
                for b in banks:
                    dve.wait_ge(sems[f"full{b}"], t.filled(b))
                size = 1 << n
                below = (flat(block_decay[0]) if n == 1 else block_decay[n - 1][:, :]).rearrange("p (b two) -> p b two", two=2)
                blocks = 4 * SEQ >> n
                if n < LEVELS:
                    dve.tensor_tensor(block_decay[n][:, :], below[:, :, 0], below[:, :, 1], ALU.mult).then_inc(sems["dve_chain"], 1)
                    dve.wait_ge(sems["dve_chain"], t.next("dve_chain"))
                q = flat(query_in).rearrange("p (b two o) -> p b two o", two=2, o=size // 2)
                k = flat(key).rearrange("p (b two o) -> p b two o", two=2, o=size // 2)
                wide = [P, blocks, size // 2]
                dve.tensor_tensor(q[:, :, 1, :], q[:, :, 1, :], below[:, :, 0].unsqueeze(2).broadcast_to(wide), ALU.mult)
                dve.tensor_tensor(k[:, :, 0, :], k[:, :, 0, :], below[:, :, 1].unsqueeze(2).broadcast_to(wide),
                                  ALU.mult).then_inc(sems["rung_ready"], 1)
                mask = level_mask[:, n - 1, :].bitcast(I32).rearrange("p (b o) -> p b o", o=size // 2)
                for s, b in enumerate(banks):
                    for h in range(4):
                        ins = dve.copy_predicated(
                            wT[:, s, h, :].rearrange("p (b two o) -> p b two o", two=2, o=size // 2)[:, :, 1, :],
                            mask, mix_bank[b][:, h * P // 2:(h + 1) * P // 2].rearrange("p (b o) -> p b o", o=size // 2))
                    ins.then_inc(sems[f"free{b}"], 1)

            def rec_out():
                t.skip(1, 2)
                dve.wait_ge(sems["sq_ready"], t.next("sq_ready"))
                dve.tensor_reduce(head_ss[:, 0:8], sq_b[:, :, :].rearrange("p t (h d) -> p (t h) d", h=4),
                                  AX.X, ALU.add).then_inc(sems["ss_ready"], 1)
                yield
                dve.wait_ge(sems["head_rs_ready"], t.next("head_rs_ready"))
                o = out_tok.rearrange("p t (h d) -> p (t h) d", h=4)
                dve.tensor_tensor(o, o, head_rs[:, 0:8].unsqueeze(2).broadcast_to([P, 8, P]), ALU.mult).then_inc(sems["dve_chain"], 1)
                dve.wait_ge(sems["dve_chain"], t.next("dve_chain"))
                dve.tensor_tensor(o, o, g_gain[:, :].unsqueeze(1).broadcast_to([P, 8, P]), ALU.mult).then_inc(sems["dve_chain"], 1)
                dve.wait_ge(sems["dve_chain"], t.next("dve_chain"))
                yield
                for s in range(TILES):
                    ins = dve.scalar_tensor_tensor(out=out_tok[:, s, :], in0=gate_b[:, s, :], scalar=rs[:, s:s + 1],
                                                   in1=out_tok[:, s, :], op0=ALU.mult, op1=ALU.mult)
                ins.then_inc(sems["gate_used"], 1)

            def recurrence_head(g):
                rec_start(g)
                yield
                rec_same()
                for n in range(1, SPLIT_LEVEL + 1):
                    yield
                    rec_level(n)

            def recurrence_tail(g):
                for n in range(SPLIT_LEVEL + 1, LEVELS + 1):
                    rec_level(n)
                    yield
                t.skip(0)
                dve.wait_ge(sems["rung_ready"], t.next("rung_ready"))
                yield
                yield from rec_out()
                yield
                plain_block(mixT, g * 4)

            dve.wait_ge(sems["full3"], t.filled(3))
            dve.tensor_copy(columns[:, 0:NORM_MIX], mix_bank[3][:, 0:NORM_MIX]).then_inc(sems["free3"], 1)
            dve.wait_ge(sems["free3"], t.value("free3"))
            gained_block(memT[0], 0, NORM_MEM)
            for _ in range(LEAD):
                split()

            def bounds_less_max():
                l0, l1 = (columns[:, LB_ROW + n * HEADS_B:LB_ROW + (n + 1) * HEADS_B] for n in range(2))
                dve.tensor_tensor(lb_work[:, 2, :], l0, l1, ALU.max).then_inc(sems["dve_chain"], 1)
                dve.wait_ge(sems["dve_chain"], t.next("dve_chain"))
                dve.tensor_tensor(lb_work[:, 0, :], l0, lb_work[:, 2, :], ALU.subtract)
                dve.tensor_tensor(lb_work[:, 1, :], l1, lb_work[:, 2, :], ALU.subtract).then_inc(sems["lb_less_max"], 1)

            def bounds():
                dve.wait_ge(sems["lb_exp"], t.next("lb_exp"))
                e0, e1, total, share = (lb_work[:, n, :] for n in range(4))
                slope, base, minus = (decay_table[:, n, :] for n in range(3))
                dve.tensor_tensor(total, e0, e1, ALU.add).then_inc(sems["dve_chain"], 1)
                dve.wait_ge(sems["dve_chain"], t.next("dve_chain"))
                dve.reciprocal(share, total).then_inc(sems["dve_chain"], 1)
                dve.wait_ge(sems["dve_chain"], t.next("dve_chain"))
                dve.tensor_tensor(e0, e0, share, ALU.mult).then_inc(sems["dve_chain"], 1)
                dve.wait_ge(sems["dve_chain"], t.next("dve_chain"))
                dve.tensor_tensor(e1, e1, share, ALU.mult).then_inc(sems["dve_chain"], 1)
                dve.wait_ge(sems["dve_chain"], t.next("dve_chain"))
                dve.tensor_tensor(total, e0, e1, ALU.add).then_inc(sems["dve_chain"], 1)
                dve.wait_ge(sems["dve_chain"], t.next("dve_chain"))
                dve.tensor_tensor(total, total, e0, ALU.subtract).then_inc(sems["dve_chain"], 1)
                dve.wait_ge(sems["dve_chain"], t.next("dve_chain"))
                dve.tensor_scalar(slope, total, -0.5, 0.5, ALU.mult, ALU.add).then_inc(sems["dve_chain"], 1)
                dve.wait_ge(sems["dve_chain"], t.next("dve_chain"))
                dve.tensor_tensor(base, total, slope, ALU.add).then_inc(sems["dve_chain"], 1)
                dve.wait_ge(sems["dve_chain"], t.next("dve_chain"))
                dve.tensor_scalar(minus, slope, -1.0, None, ALU.mult).then_inc(sems["dve_chain"], 1)
                dve.wait_ge(sems["dve_chain"], t.next("dve_chain"))

            def angles():
                dve.wait_ge(sems["tables_in"], t.next("tables_in", 5 * 16))
                dve.wait_ge(sems["freq_ready"], t.next("freq_ready"))
                dve.tensor_copy(turn[:, :, 0:1], pos_int[:, :].unsqueeze(2)).then_inc(sems["dve_chain"], 1)
                dve.wait_ge(sems["dve_chain"], t.next("dve_chain"))
                dve.tensor_tensor(ang[:, :, :], turn[:, :, 0:1].broadcast_to([P, TILES, ROT]),
                                  freq[:, :].unsqueeze(1).broadcast_to([P, TILES, ROT]), ALU.mult).then_inc(sems["dve_chain"], 1)
                dve.wait_ge(sems["dve_chain"], t.next("dve_chain"))
                for whole in (2 * np.pi * 1024, 2 * np.pi):
                    yield
                    magic = 1.5 * 2 ** 23
                    dve.tensor_scalar(turn[:, :, :], ang[:, :, :], 1.0 / whole, magic, ALU.mult, ALU.add).then_inc(sems["dve_chain"], 1)
                    dve.wait_ge(sems["dve_chain"], t.next("dve_chain"))
                    dve.tensor_scalar(turn[:, :, :], turn[:, :, :], magic, None, ALU.subtract).then_inc(sems["dve_chain"], 1)
                    dve.wait_ge(sems["dve_chain"], t.next("dve_chain"))
                    yield
                    for part in short_parts(whole):
                        dve.scalar_tensor_tensor(out=ang[:, :, :], in0=turn[:, :, :], scalar=-part,
                                                 in1=ang[:, :, :], op0=ALU.mult, op1=ALU.add).then_inc(sems["dve_chain"], 1)
                        dve.wait_ge(sems["dve_chain"], t.next("dve_chain"))
                yield
                dve.tensor_scalar(ang[:, :, :], ang[:, :, :], 3.1415925, -3.1415925, ALU.min,
                                  ALU.max).then_inc(sems["angles_ready"], 1)
                dve.tensor_scalar(minus_sink[:, :], sink[:, :], -1.0, None, ALU.mult)
                dve.tensor_scalar(g_gain[:, :], g_gain[:, :], 0.5, None, ALU.mult).then_inc(sems["dve_chain"], 1)
                dve.wait_ge(sems["dve_chain"], t.next("dve_chain"))

            def cosines():
                dve.wait_ge(sems["sines_ready"], t.next("sines_ready"))
                dve.tensor_tensor(cos[:, :, :], turn[:, :, :], turn[:, :, :], ALU.mult).then_inc(sems["dve_chain"], 1)
                dve.wait_ge(sems["dve_chain"], t.next("dve_chain"))
                dve.tensor_scalar(cos[:, :, :], cos[:, :, :], -2.0, 1.0, ALU.mult, ALU.add).then_inc(sems["dve_chain"], 1)
                dve.wait_ge(sems["dve_chain"], t.next("dve_chain"))

            for i in pieces(8):
                if i in (1, 2, 4):
                    gained_block(memT[0], (1, 2, 4).index(i) * 4 + 4, NORM_MEM)
                if i == 6:
                    dve.wait_ge(sems["full3"], t.filled(3))
                    dve.tensor_copy(columns[:, NORM_MIX:ROWS], mix_bank[3][:, 0:ROWS - NORM_MIX]).then_inc(sems["free3"], 1)
            pass_unit(0)
            norm = norm_memory_heads(tanh_ff, vm_b)
            for i in pieces(8):
                if i % 2 == 0:
                    gained_block(memT[1], i * 2, NORM_MEM + KT)
                advance(norm, [1, 3], i)
                if i == 5:
                    dve.wait_ge(sems["free3"], t.value("free3"))
                    bounds_less_max()
            t.skip(0, 1)
            pass_unit(1)
            for i in pieces(8):
                if i % 2 == 0:
                    gained_block(hT, i * 2, NORM_MIX)
            pass_unit(0)
            norm = norm_memory_heads(tanh_ff, vm_b)
            angle_steps = angles()
            for i in pieces(8):
                advance(norm, [0, 1], i)
                advance(angle_steps, [2, 3, 4, 5, 6, 7], i)
            t.skip(0, 1)
            pass_unit(1)

            def x_add(pair, block):
                dve.wait_ge(sems["piece_used"], unit_done(pair))
                for s in range(TILES):
                    part = x_tok[:, s, block * COLS:(block + 1) * COLS]
                    dve.tensor_tensor(part, unit_bank[2 * pair + s][:, :], part, ALU.add).then_inc(sems[f"unit_free{pair}"], 1)

            def projection_ffn(layer, mix, pair):
                other = 1 - pair
                row = NORM_FFN + layer * KT
                for i in pieces(16):
                    if i == 14:
                        x_add(pair, 0)
                    mix(i)
                x_add(other, 1)
                for i in pieces(8):
                    if i in (1, 4):
                        gained_block(hT, (1, 4).index(i) * 4, row)
                x_add(pair, 2)
                for i in pieces(8):
                    if i == 1:
                        gained_block(hT, 8, row)
                x_add(other, 3)

                def chunk(j):
                    for i in pieces(8):
                        if j is None and i == 2:
                            gained_block(hT, 12, row)
                        if j is not None and i == 1:
                            plain_block(gT, (j - 1) * 4)
                    if j is None:
                        dve.wait_ge(sems["rs_ready"], t.next("rs_ready"))
                    t.move(f"unit_free{pair}", TILES)
                    for s in range(TILES):
                        dve.wait_ge(sems["tanh_ff_ready"], t.next("tanh_ff_ready"))
                        dve.scalar_tensor_tensor(out=tanh_ff[:, s, :], in0=tanh_ff[:, s, :], scalar=1.0,
                                                 in1=unit_bank[2 * pair + s][:, :], op0=ALU.add,
                                                 op1=ALU.mult).then_inc(sems[f"unit_free{pair}"], 1)
                    for i in pieces(8):
                        pass
                    dve.wait_ge(sems["piece_used"], unit_done(other))
                    dve.wait_ge(sems[f"unit_free{pair}"], t.value(f"unit_free{pair}"))
                    for s in range(TILES):
                        dve.scalar_tensor_tensor(out=act_ff[:, s, :], in0=unit_bank[2 * other + s][:, :],
                                                 scalar=half_rs2[:, s:s + 1], in1=tanh_ff[:, s, :], op0=ALU.mult,
                                                 op1=ALU.mult).then_inc(sems[f"unit_free{other}"], 1)

                chunk(None)
                with t.loop(1, CHUNKS_FF, per_chunk) as j:
                    chunk(j)
                for c in range(BLOCKS):
                    for i in pieces(len(FF_KTS), tail=layer == 1 and c == BLOCKS - 1):
                        if c == 0 and i == 1:
                            plain_block(gT, FT - 4)
                        if layer == 0 and c > 0 and i == 2:
                            gained_block(hT, (c - 1) * 4, NORM_MIX + KT)
                    x_add((pair, other)[c % 2], c)

            def slots(n):
                return {"hi_ready": n, "split": n, "at": n}

            def banks(*counts):
                return {f"{k}{b}": n for b, n in enumerate(counts) if n for k in ("full", "free")}

            per_chunk = slots(16) | banks(1, 1) | {"unit_free0": 2, "unit_free1": 2, "tanh_ff_ready": 2, "hi_block": 2}

            dve.wait_ge(sems["rs_ready"], t.next("rs_ready"))
            for i in pieces(8):
                if i == 1:
                    cosines()
                if i == 3:
                    bounds()
            pass_unit(0)

            def window_keys():
                yield from norm_window_heads(kv_a, sq_a, k_gain, KV_A, "dve_chain")
                yield
                kv_v = kv_a[:, :, KV_A * HD_A:]
                keys = kv_a[:, :, 0:KV_A * HD_A].rearrange("p t (h d) -> p t h d", d=HD_A)
                dve.tensor_copy(v_mid[0:P // 2, :], kv_v[P // 2:P, 0, :])
                dve.tensor_copy(v_mid[P // 2:P, :], kv_v[0:P // 2, 1, :])
                dve.tensor_copy(k_twice[:, :, :, 0, :], keys)
                dve.tensor_copy(k_twice[:, :, :, 1, :], keys).then_inc(sems["heads_ready"], 1)
                dve.wait_ge(sems["heads_ready"], t.next("heads_ready"))

            norm = window_keys()
            for i in pieces(8):
                advance(norm, NORM_STEPS + [4], i)
            t.skip(0, 1)
            pass_unit(1)

            norm, head = norm_memory_heads(qm_a, sq_a), attention_head(False, pT_a)
            for i in pieces(8):
                advance(norm, [0, 1], i)
                advance(head, HEAD_STEPS, i)
            pass_unit(0)

            def windows(norm, tail, head, i):
                advance(head, HEAD_STEPS, i)
                advance(tail, TAIL_STEPS, i)
                advance(norm, NORM_STEPS, i)

            tail = attention_tail(False, pT_a, mix_a, 12)
            for g in range(GROUPS - 1):
                norm, head = norm_window_heads(q_a, sq_a, q_gain, GROUP_A, "heads_ready"), attention_head(True, pT_a, g)
                for i in pieces(8):
                    windows(norm, tail, head, i)
                pass_unit(1 - g)
                tail = attention_tail(True, pT_a, mix_a, g * 4)
            norm, head = norm_window_heads(q_a, sq_a, q_gain, GROUP_A, "heads_ready"), attention_head(True, pT_a, 2)
            last_tail = attention_tail(True, pT_a, mix_a, 8)

            def last_windows(i):
                windows(norm, tail, head, i)
                advance(last_tail, LAST_TAIL_STEPS, i)

            projection_ffn(0, last_windows, 1)

            def group_b(g, before, positions):
                head = recurrence_head(g)
                for u in range(4):
                    for i in pieces(8):
                        advance(before, positions, 8 * u + i)
                        advance(head, REC_HEAD_STEPS, 8 * u + i)
                    pass_unit(u % 2)
                for s in range(TILES):
                    dve.wait_ge(sems["tanh_gate_ready"], t.next("tanh_gate_ready"))
                    dve.scalar_tensor_tensor(out=gate_b[:, s, :], in0=gate_b[:, s, :], scalar=1.0,
                                             in1=unit_bank[2 + s][:, :], op0=ALU.add,
                                             op1=ALU.mult).then_inc(sems["unit_free1"], 1)

            for i in pieces(8):
                if i == 2:
                    gained_block(hT, 12, NORM_MIX + KT)
            dve.wait_ge(sems["rs_ready"], t.next("rs_ready"))
            pass_unit(1)
            group_b(0, chain(norm_memory_heads(qm_b, sq_b), attention_head(False, pT_b),
                             attention_tail(False, pT_b, out_tok, 12)), [0, 1] + MEMORY_STEPS)
            with t.loop(1, GROUPS, slots(32) | banks(7, 7, 6, 5)
                        | {"unit_free0": 4, "unit_free1": 4, "tanh_q_ready": 2, "rung_ready": 8, "sq_ready": 1,
                           "head_rs_ready": 1, "hi_block": 2, "tanh_gate_ready": 2, "dve_chain": 10}) as g:
                group_b(g, recurrence_tail(g - 1), REC_NORM_TAIL_STEPS)
            tail = recurrence_tail(2)
            projection_ffn(1, lambda i: advance(tail, REC_NORM_TAIL_STEPS, i), 0)

        @block.tensor
        def _(pe):
            t = Turns(pe, sems)
            slot = [0]

            def products(*units):
                i = 0
                for stationary, pair, kts, opens, closes, cols in units:
                    for n, kt in enumerate(kts):
                        yield i
                        if opens and n == 0 and t.any(f"unit_free{pair}"):
                            pe.wait_ge(sems[f"unit_free{pair}"], t.value(f"unit_free{pair}"))
                        s = slot[0] % RING
                        slot[0] += 1
                        pe.wait_ge(sems["lo_ready"], t.next("lo_ready"))
                        for j in range(2):
                            for tile in range(TILES):
                                x_hi, x_lo = (m[:, kt + j, tile * P:(tile + 1) * P] for m in stationary)
                                products = ((x_hi, w_hi), (x_hi, w_lo), (x_lo, w_hi))
                                for m, (a, b) in enumerate(products):
                                    ins = pe.matmul(unit_bank[2 * pair + tile][:, 0:cols], a, b[:, s, j, 0:cols],
                                                    start=opens and n == 0 and j == 0 and m == 0,
                                                    stop=closes and n == len(kts) - 1 and j == 1 and m == 2)
                        ins.then_inc(sems["piece_used"], 1)
                        i += 1
                    if closes:
                        t.move(f"unit_free{pair}", TILES)

            def unit(stationary, pair, kts=ALL_KTS, opens=True, closes=True, cols=COLS):
                return (stationary, pair, kts, opens, closes, cols)

            def settled(*banks):
                for b in banks:
                    pe.wait_ge(sems[f"free{b}"], t.value(f"free{b}"))

            def turn_tile(src, b, count=4, width=P):
                if t.any(f"free{b}"):
                    pe.wait_ge(sems[f"free{b}"], t.value(f"free{b}"))
                t.move(f"free{b}")
                for n in range(count):
                    ins = pe.transpose(mix_bank[b][:, n * P:(n + 1) * P], src[:, n * width:(n + 1) * width], ident[:, :])
                ins.then_inc(sems[f"full{b}"], 1)

            def turn_block(src):
                for s in range(TILES):
                    turn_tile(src[:, s, :], s)

            def x_block(c):
                turn_block(x_tok[:, :, c * COLS:(c + 1) * COLS])

            def attention(tile, qT, probs, pT, mix, keysT=None, vals=None, g=None):
                window = g is not None

                def turn():
                    pe.wait_ge(sems["heads_ready"], t.next("heads_ready"))
                    turn_block(tile)

                def scores(s):
                    if s == 0:
                        settled(0, 1)
                    for b in (2, 3):
                        if t.any(f"free{b}"):
                            pe.wait_ge(sems[f"free{b}"], t.value(f"free{b}"))
                        t.move(f"free{b}")
                        if not window:
                            for n in range(2):
                                h = 2 * n + b - 2
                                ins = pe.matmul(mix_bank[b][:, n * N_MEM:(n + 1) * N_MEM], qT[:, h, s * P:(s + 1) * P],
                                                keysT[:, h, :], start=True, stop=True)
                            ins.then_inc(sems[f"full{b}"], 1)
                            continue
                        for n in range(4):
                            h = 2 * n + b - 2
                            r = slice((b - 2) * HD_A, (b - 1) * HD_A)
                            if s == 0:
                                ins = pe.matmul(mix_bank[b][:, n * P:(n + 1) * P], qT[r, h // 2, 0:P], kT[r, g, 0:P],
                                                start=True, stop=True)
                                continue
                            pe.matmul(mix_bank[b][:, n * P:(n + 1) * P], qT[r, h // 2, P:2 * P], kT[r, g, P:2 * P],
                                      start=True, stop=True)
                            ins = pe.matmul(mix_bank[b][0:64, n * P:(n + 1) * P], qT[r, h // 2, P:P + 64],
                                            kT[r, g, 64:64 + P], start=True, stop=True)
                        if s == 0:
                            r = slice((b - 2) * HD_A, (b - 2) * HD_A + 1)
                            ins = pe.matmul(mix_bank[b][0:P // 2, :].rearrange("p (h k) -> p h k", h=4)[:, :, P // 2:P],
                                            ones_row[r, :], masked_row[r, :, :], start=True, stop=True)
                        ins.then_inc(sems[f"full{b}"], 1)

                def turn_probs():
                    settled(2, 3)
                    turn_tile(probs[:, 0:4 * P], 0)
                    turn_tile(probs[:, 4 * P:8 * P], 1)

                def weighted(s):
                    settled(0, 1)
                    t.move("free0")
                    if not window:
                        for h in range(4):
                            for m in range(TILES):
                                ins = pe.matmul(mix_bank[0][:, h * P:(h + 1) * P], pT[:, 2 * h + m, :],
                                                vals[:, m, h * P:(h + 1) * P], start=m == 0, stop=m == TILES - 1)
                    else:
                        d = slice(g * HD_A, (g + 1) * HD_A)
                        kv_v = kv_a[:, :, KV_A * HD_A:]
                        window_v = (kv_v[:, 0, d], v_mid[:, d], kv_v[:, 1, d])
                        for h in range(GROUP_A):
                            cols = slice(h * HD_A, (h + 1) * HD_A)
                            if s == 0:
                                ins = pe.matmul(mix_bank[0][:, cols], pT[:, h, :], window_v[0], start=True, stop=True)
                                continue
                            for c in range(2):
                                ins = pe.matmul(mix_bank[0][c * 64:(c + 1) * 64, cols], pT[:, h, c * 64:(c + 1) * 64],
                                                window_v[1 + c], start=True, stop=True)
                    ins.then_inc(sems["full0"], 1)

                def turn_mix():
                    settled(0)
                    turn_block(mix)

                def head():
                    turn()
                    yield
                    scores(0)
                    yield
                    turn_probs()
                    scores(1)

                def tail():
                    weighted(0)
                    yield
                    turn_probs()
                    yield
                    weighted(1)
                    yield
                    turn_mix()

                return head(), tail()

            def recurrence():
                def start():
                    pe.wait_ge(sems["unit_free0"], t.value("unit_free0"))
                    pe.wait_ge(sems["unit_free1"], t.value("unit_free1"))
                    turn_block(q_b)
                    turn_tile(z_b[:, 0, :], 2)
                    turn_tile(z_b[:, 1, :], 3)

                def same():
                    pe.wait_ge(sems["rung_ready"], t.next("rung_ready"))
                    for s in range(TILES):
                        if t.any(f"free{s}"):
                            pe.wait_ge(sems[f"free{s}"], t.value(f"free{s}"))
                        t.move(f"free{s}")
                        for h in range(4):
                            ins = pe.matmul(mix_bank[s][:, h * P:(h + 1) * P], key[:, h, s * P:(s + 1) * P],
                                            query[:, h, s * P:(s + 1) * P], start=True, stop=True)
                        ins.then_inc(sems[f"full{s}"], 1)

                def level(n):
                    if n > 1:
                        pe.wait_ge(sems["rung_ready"], t.next("rung_ready"))
                    size = 1 << n
                    for s in range(TILES):
                        b = (2 if n % 2 else 0) + s
                        if t.any(f"free{b}"):
                            pe.wait_ge(sems[f"free{b}"], t.value(f"free{b}"))
                        t.move(f"free{b}")
                        for h in range(4):
                            late = query_in[:, h, s * P:(s + 1) * P].rearrange("p (b two o) -> p b two o", two=2, o=size // 2)[:, :, 1, :]
                            ins = pe.matmul(mix_bank[b][:, h * P // 2:(h + 1) * P // 2], key[:, h, s * P:(s + 1) * P],
                                            late, start=True, stop=True)
                        ins.then_inc(sems[f"full{b}"], 1)

                def cross():
                    pe.wait_ge(sems["rung_ready"], t.next("rung_ready"))
                    if t.any("free0"):
                        pe.wait_ge(sems["free0"], t.value("free0"))
                    t.move("free0")
                    for h in range(4):
                        ins = pe.matmul(mix_bank[0][:, h * P:(h + 1) * P], key[:, h, 0:P], query_in[:, h, P:2 * P],
                                        start=True, stop=True)
                    ins.then_inc(sems["full0"], 1)

                def outputs():
                    settled(0, 1, 2, 3)
                    if t.any("free1"):
                        pe.wait_ge(sems["free1"], t.value("free1"))
                    t.move("free1")
                    for h in range(4):
                        ins = pe.matmul(mix_bank[1][:, h * P:(h + 1) * P], wT[:, 0, h, :], v_b[:, 0, h * P:(h + 1) * P],
                                        start=True, stop=True)
                    ins.then_inc(sems["full1"], 1)
                    if t.any("free2"):
                        pe.wait_ge(sems["free2"], t.value("free2"))
                    t.move("free2")
                    for h in range(4):
                        pe.matmul(mix_bank[2][:, h * P:(h + 1) * P], wT_cross[:, h, :], v_b[:, 0, h * P:(h + 1) * P],
                                  start=True, stop=False)
                        ins = pe.matmul(mix_bank[2][:, h * P:(h + 1) * P], wT[:, 1, h, :], v_b[:, 1, h * P:(h + 1) * P],
                                        start=False, stop=True)
                    ins.then_inc(sems["full2"], 1)

                def turn_mix():
                    pe.wait_ge(sems["gate_used"], t.next("gate_used"))
                    turn_block(out_tok)

                def head():
                    start()
                    yield
                    same()
                    for n in range(1, SPLIT_LEVEL + 1):
                        yield
                        level(n)

                def tail():
                    for n in range(SPLIT_LEVEL + 1, LEVELS + 1):
                        level(n)
                        yield
                    cross()
                    yield
                    outputs()
                    yield
                    turn_mix()

                return head(), tail()

            pe.wait_ge(sems["ident_ready"], t.next("ident_ready"))
            pe.wait_ge(sems["first_rows_in"], t.next("first_rows_in", 16))
            if t.any("free3"):
                pe.wait_ge(sems["free3"], t.value("free3"))
            t.move("free3")
            pe.transpose(mix_bank[3][:, 0:NORM_MIX], first_rows[0:NORM_MIX, :],
                         ident[0:NORM_MIX, 0:NORM_MIX]).then_inc(sems["full3"], 1)

            def mem_block(c):
                turn_block(mem_tok[:, :, c * COLS:(c + 1) * COLS])

            def turn_keys():
                pe.wait_ge(sems["heads_ready"], t.next("heads_ready"))
                turn_block(tanh_ff)

            pe.wait_ge(sems["mem_in0"], t.next("mem_in0", 16))
            mem_block(0)
            for i in products(unit(memT[0], 0)):
                if i in (0, 2, 4, 6):
                    settled(0, 1)
                if i in (1, 2, 4):
                    c = (1, 2, 4).index(i) + 1
                    pe.wait_ge(sems[f"mem_in{c}"], t.next(f"mem_in{c}", 16))
                    mem_block(c)
                if i == 6:
                    pe.wait_ge(sems["rows_in"], t.next("rows_in", 5 * 16))
                    pe.wait_ge(sems["free3"], t.value("free3"))
                    t.move("free3")
                    n = ROWS - NORM_MIX
                    pe.transpose(mix_bank[3][:, 0:n], rows[0:n, :], ident[0:n, 0:n]).then_inc(sems["full3"], 1)
            for i in products(unit(memT[0], 1)):
                if i % 2 == 0:
                    mem_block(i // 2)
                if i == 7:
                    turn_keys()
            settled(0, 1)
            for i in products(unit(memT[1], 0)):
                if i % 2 == 0:
                    pe.wait_ge(sems[f"x_in{i // 2}"], t.next(f"x_in{i // 2}", 16))
                    x_block(i // 2)
            for i in products(unit(memT[1], 1)):
                if i == 4:
                    turn_keys()
            settled(0, 1)

            for i in products(unit(hT, 0, cols=2 * KV_A * HD_A)):
                pass

            def turn_window_keys():
                pe.wait_ge(sems["heads_ready"], t.next("heads_ready"))
                for s in range(TILES):
                    turn_tile(k_twice[:, s, :, :, :].rearrange("p h a d -> p (h a d)"), s, KV_A)

            for i in products(unit(hT, 1)):
                if i == 4:
                    turn_window_keys()
            pe.wait_ge(sems["mask_rows_ready"], t.next("mask_rows_ready"))
            head, tail = attention(qm_a, qT_a, p_a, pT_a, mix_a, kmT[0], vm[0])
            for i in products(unit(hT, 0)):
                advance(head, HEAD_STEPS, i)
            for g in range(GROUPS - 1):
                head, next_tail = attention(q_a, qT_a, p_a, pT_a, mix_a, g=g)
                for i in products(unit(hT, 1 - g)):
                    advance(head, HEAD_STEPS, i)
                    advance(tail, TAIL_STEPS, i)
                tail = next_tail

            def banks(*counts):
                return {f"free{b}": n for b, n in enumerate(counts) if n}

            def projection_ffn(layer, mix, pair):
                other = 1 - pair
                settled(0, 1)
                parts = [unit(mixT, p, kts, opens=n == 0, closes=n == 2) for n, kts in enumerate(MIXED_KTS) for p in (pair, other)]
                for i in products(*parts):
                    if i == 8:
                        settled(0, 1)
                    mix(i)
                    if i == 12:
                        settled(0, 1)
                for i in products(unit(mixT, pair)):
                    if i == 1:
                        x_block_after(pair, other, 0)
                    if i == 4:
                        x_block(1)
                for i in products(unit(mixT, other)):
                    if i == 1:
                        x_block_after(pair, other, 2)
                for i in products(unit(hT, pair), unit(hT, other)):
                    if i in (0, 6):
                        settled(0, 1)
                    if i == 2:
                        x_block_after(pair, other, 3)

                def act_block():
                    pe.wait_ge(sems[f"unit_free{other}"], t.value(f"unit_free{other}"))
                    turn_block(act_ff)

                with t.loop(1, CHUNKS_FF, banks(1, 1) | {"lo_ready": 16, "unit_free0": 2, "unit_free1": 2}):
                    for i in products(unit(hT, pair), unit(hT, other)):
                        if i == 1:
                            act_block()
                for c in range(BLOCKS):
                    for i in products(unit(gT, (pair, other)[c % 2], FF_KTS)):
                        if c == 0 and i == 1:
                            act_block()
                        if c == 0 and i == 6:
                            settled(0, 1)
                        if layer == 0 and c > 0 and i == 2:
                            x_block_after(pair, other, c - 1)

            def x_block_after(pair, other, c):
                pe.wait_ge(sems[f"unit_free{pair}"], t.value(f"unit_free{pair}"))
                pe.wait_ge(sems[f"unit_free{other}"], t.value(f"unit_free{other}"))
                x_block(c)

            head, last_tail = attention(q_a, qT_a, p_a, pT_a, mix_a, g=GROUPS - 1)

            def last_windows(i):
                advance(head, HEAD_STEPS, i)
                advance(tail, TAIL_STEPS, i)
                advance(last_tail, LAST_TAIL_STEPS, i)

            projection_ffn(0, last_windows, 1)

            for i in products(unit(hT, 1)):
                if i == 2:
                    x_block_after(0, 1, BLOCKS - 1)
                if i == 6:
                    settled(0, 1)
            group = [unit(hT, 0), unit(hT, 1), unit(hT, 0), unit(hT, 1)]
            before = chain(*attention(qm_b, qT_b, p_b, pT_b, out_tok, kmT[1], vm[1]))
            head, tail = recurrence()
            for i in products(*group):
                advance(before, MEMORY_STEPS, i)
                advance(head, REC_HEAD_STEPS, i)
            with t.loop(1, GROUPS, banks(7, 7, 6, 5) | {"lo_ready": 32, "unit_free0": 4, "unit_free1": 4,
                                                        "rung_ready": 8, "gate_used": 1}):
                head, next_tail = recurrence()
                for i in products(*group):
                    advance(tail, REC_TAIL_STEPS, i)
                    advance(head, REC_HEAD_STEPS, i)
            projection_ffn(1, lambda i: advance(next_tail, REC_TAIL_STEPS, i), 0)


_INS = ["x", "mem", "positions", "norm_mix", "norm_ffn", "norm_mem", "w_in_a", "q_norm_a", "k_norm_a", "sinks_a",
        "w_in_b", "lb_logits", "g_norm_b", "w_mem_kv", "q_norm_m", "k_norm_m", "w_o", "w_gate_up", "w_down"]


def kernel(**inputs):
    import concourse.bacc as bacc
    from concourse.bass_utils import run_bass_kernel_spmd

    nc = bacc.Bacc("TRN2", target_bir_lowering=False, num_devices=1)
    arrays, args = {}, []
    for name in _INS:
        a = np.ascontiguousarray(inputs[name])
        arrays[f"in_{name}"] = a
        args.append(nc.dram_tensor(f"in_{name}", a.shape, mybir.dt.from_np(a.dtype), kind="ExternalInput").ap())
    args.append(nc.dram_tensor("out_trunk", (1, SEQ, D), F32, kind="ExternalOutput").ap())
    trunk(nc, *args)
    r = run_bass_kernel_spmd(nc, [arrays], core_ids=[0])
    return r.results[0]["out_trunk"]
```
